# Optimizing a Trainium2 kernel written in Bass

```python
import jax, jax.numpy as jnp
from jax import lax
import numpy as np

D_MODEL = 1024
BATCH = 1
SEQ = 256
DEPTH = 2

N_MEM = 256
RMS_EPS = 1e-6
N_SUBNORMS = 6

ML_HEADS = 4
ML_QK_DIM = D_MODEL // 2 // ML_HEADS
ML_V_DIM = D_MODEL // ML_HEADS
ML_CHUNK = 64
ML_GATE_CAP = 15.0
ML_IN_WIDTH = 2 * ML_HEADS * ML_QK_DIM + 2 * D_MODEL + 2 * ML_HEADS

SB_HEADS = 16
SB_HEAD_DIM = D_MODEL // SB_HEADS
SB_BLOCK = 128

XA_HEADS = 4
XA_HEAD_DIM = D_MODEL // XA_HEADS

D_FF = -(-8 * D_MODEL // (3 * 256)) * 256

N_ML_LAYERS = (DEPTH + 1) // 2
N_SB_LAYERS = DEPTH // 2


def rms_norm(x, gain):
    x32 = x.astype(jnp.float32)
    y = x32 * lax.rsqrt(jnp.mean(x32 * x32, axis=-1, keepdims=True) + RMS_EPS)
    return (y * gain.astype(jnp.float32)).astype(x.dtype)

def mlstm_mixer(h, w_in, b_gate, head_gain, w_out):
    B, S, _ = h.shape
    H, dk, dv, L = ML_HEADS, ML_QK_DIM, ML_V_DIM, ML_CHUNK
    nc = S // L
    qk = H * dk
    proj = h @ w_in
    q, k, v, o, gates = jnp.split(proj, [qk, 2 * qk, 2 * qk + D_MODEL, 2 * qk + 2 * D_MODEL], axis=-1)
    gates = gates.astype(jnp.float32) + b_gate.astype(jnp.float32)
    gates = ML_GATE_CAP * jnp.tanh(gates / ML_GATE_CAP)
    ig = gates[..., :H]
    lf = jax.nn.log_sigmoid(gates[..., H:])

    def to_chunks(t, d):
        return t.astype(jnp.float32).reshape(B, nc, L, H, d).transpose(1, 0, 3, 2, 4)

    def gate_chunks(t):
        return t.reshape(B, nc, L, H).transpose(1, 0, 3, 2)

    qc = to_chunks(q, dk)
    kc = to_chunks(k, dk) * (dk ** -0.5)
    vc = to_chunks(v, dv)
    igc, lfc = gate_chunks(ig), gate_chunks(lf)
    causal = jnp.tril(jnp.ones((L, L), dtype=bool))

    def step(carry, inp):
        C, n, m = carry
        qb, kb, vb, igb, lfb = inp
        b = jnp.cumsum(lfb, axis=-1)
        log_d = jnp.where(causal, b[..., :, None] - b[..., None, :] + igb[..., None, :], -jnp.inf)
        m_inter = b + m[..., None]
        m_t = jnp.maximum(jnp.max(log_d, axis=-1), m_inter)
        d = jnp.exp(log_d - m_t[..., None])
        s = jnp.einsum('bhtd,bhsd->bhts', qb, kb) * d
        inter = jnp.exp(m_inter - m_t)
        num = jnp.einsum('bhts,bhsv->bhtv', s, vb) + inter[..., None] * jnp.einsum('bhvd,bhtd->bhtv', C, qb)
        den = jnp.sum(s, axis=-1) + inter * jnp.einsum('bhd,bhtd->bht', n, qb)
        h_out = num / jnp.maximum(jnp.abs(den), jnp.exp(-m_t))[..., None]
        b_last = b[..., -1]
        g = b_last[..., None] - b + igb
        m_new = jnp.maximum(b_last + m, jnp.max(g, axis=-1))
        w = jnp.exp(g - m_new[..., None])
        decay = jnp.exp(b_last + m - m_new)
        C = decay[..., None, None] * C + jnp.einsum('bhs,bhsv,bhsd->bhvd', w, vb, kb)
        n = decay[..., None] * n + jnp.einsum('bhs,bhsd->bhd', w, kb)
        return (C, n, m_new), h_out

    init = (jnp.zeros((B, H, dv, dk), jnp.float32),
            jnp.zeros((B, H, dk), jnp.float32),
            jnp.zeros((B, H), jnp.float32))
    _, hs = lax.scan(step, init, (qc, kc, vc, igc, lfc))
    hs = hs.transpose(1, 0, 3, 2, 4).reshape(B, S, H, dv)
    hs = rms_norm(hs, head_gain.reshape(H, dv))
    og = jax.nn.sigmoid(o.astype(jnp.float32)).reshape(B, S, H, dv)
    out = (hs * og).reshape(B, S, D_MODEL).astype(h.dtype)
    return out @ w_out

def stick_breaking_mixer(h, w_qkv, w_out):
    B, S, _ = h.shape
    H, dh = SB_HEADS, SB_HEAD_DIM
    qkv = (h @ w_qkv).reshape(B, S, 3, H, dh).astype(jnp.float32)
    q = qkv[:, :, 0].transpose(0, 2, 1, 3)
    k = qkv[:, :, 1].transpose(0, 2, 1, 3)
    v = qkv[:, :, 2].transpose(0, 2, 1, 3)
    scale = dh ** -0.5
    outs = []
    for blk in range(S // SB_BLOCK):
        q0 = blk * SB_BLOCK
        kend = q0 + SB_BLOCK
        qb = q[:, :, q0:kend]
        kb = k[:, :, :kend]
        vb = v[:, :, :kend]
        z = jnp.einsum('bhtd,bhsd->bhts', qb, kb) * scale
        t_idx = q0 + jnp.arange(SB_BLOCK)[:, None]
        s_idx = jnp.arange(kend)[None, :]
        strict = s_idx < t_idx
        log_1m = jnp.where(strict, jax.nn.log_sigmoid(-z), 0.0)
        suffix = lax.cumsum(log_1m, axis=3, reverse=True) - log_1m
        a = jnp.where(strict, jnp.exp(jax.nn.log_sigmoid(z) + suffix), 0.0)
        outs.append(jnp.einsum('bhts,bhsd->bhtd', a, vb))
    o = jnp.concatenate(outs, axis=2)
    o = o.transpose(0, 2, 1, 3).reshape(B, S, D_MODEL).astype(h.dtype)
    return o @ w_out

def memory_cross_attention(h, mem_n, w_q, w_kv, w_o):
    B, S, _ = h.shape
    q = (h @ w_q).reshape(B, S, XA_HEADS, XA_HEAD_DIM)
    kv = (mem_n @ w_kv).reshape(B, mem_n.shape[1], 2, XA_HEADS, XA_HEAD_DIM)
    k, v = kv[:, :, 0], kv[:, :, 1]
    s = jnp.einsum('bthd,bmhd->bhtm', q, k).astype(jnp.float32) * (XA_HEAD_DIM ** -0.5)
    p = jax.nn.softmax(s, axis=-1).astype(v.dtype)
    o = jnp.einsum('bhtm,bmhd->bthd', p, v).reshape(B, S, D_MODEL)
    return o @ w_o

def swiglu_ffn(h, w_gate_up, w_down):
    gate, up = jnp.split(h @ w_gate_up, 2, axis=-1)
    return (jax.nn.silu(gate) * up) @ w_down

def first_inputs(seed: int = 0) -> dict:
    key = jax.random.key(seed)
    ks = jax.random.split(key, 16)

    def w(k, shape, fan_in):
        return jax.random.normal(k, shape, jnp.float32) * (fan_in ** -0.5)

    x = jax.random.normal(ks[0], (BATCH, SEQ, D_MODEL), jnp.float32)
    mem = jax.random.normal(ks[1], (BATCH, N_MEM, D_MODEL), jnp.float32)
    mem_norm_gain = 1.0 + 0.02 * jax.random.normal(ks[2], (D_MODEL,), jnp.float32)
    norm_gains = 1.0 + 0.02 * jax.random.normal(ks[3], (DEPTH, N_SUBNORMS, D_MODEL), jnp.float32)
    ml_w_in = w(ks[4], (N_ML_LAYERS, D_MODEL, ML_IN_WIDTH), D_MODEL)
    kb1, kb2 = jax.random.split(ks[5])
    b_in = 0.01 * jax.random.normal(kb1, (N_ML_LAYERS, ML_HEADS), jnp.float32)
    b_f = jnp.linspace(3.0, 6.0, ML_HEADS)[None, :] + 0.01 * jax.random.normal(kb2, (N_ML_LAYERS, ML_HEADS), jnp.float32)
    ml_b_gate = jnp.concatenate([b_in, b_f], axis=-1)
    ml_head_gain = 1.0 + 0.02 * jax.random.normal(ks[6], (N_ML_LAYERS, D_MODEL), jnp.float32)
    ml_w_out = w(ks[7], (N_ML_LAYERS, D_MODEL, D_MODEL), D_MODEL)
    sb_w_qkv = w(ks[8], (N_SB_LAYERS, D_MODEL, 3 * D_MODEL), D_MODEL)
    sb_w_out = w(ks[9], (N_SB_LAYERS, D_MODEL, D_MODEL), D_MODEL)
    xa_w_q = w(ks[10], (DEPTH, D_MODEL, D_MODEL), D_MODEL)
    xa_w_kv = w(ks[11], (DEPTH, D_MODEL, 2 * D_MODEL), D_MODEL)
    xa_w_o = w(ks[12], (DEPTH, D_MODEL, D_MODEL), D_MODEL)
    ffn_w_gate_up = w(ks[13], (DEPTH, D_MODEL, 2 * D_FF), D_MODEL)
    ffn_w_down = w(ks[14], (DEPTH, D_FF, D_MODEL), D_FF)
    return {"x": x, "mem": mem, "mem_norm_gain": mem_norm_gain, "norm_gains": norm_gains,
            "ml_w_in": ml_w_in, "ml_b_gate": ml_b_gate, "ml_head_gain": ml_head_gain, "ml_w_out": ml_w_out,
            "sb_w_qkv": sb_w_qkv, "sb_w_out": sb_w_out,
            "xa_w_q": xa_w_q, "xa_w_kv": xa_w_kv, "xa_w_o": xa_w_o,
            "ffn_w_gate_up": ffn_w_gate_up, "ffn_w_down": ffn_w_down}

def first_block(x, mem, mem_norm_gain, norm_gains, ml_w_in, ml_b_gate, ml_head_gain, ml_w_out,
              sb_w_qkv, sb_w_out, xa_w_q, xa_w_kv, xa_w_o, ffn_w_gate_up, ffn_w_down):
    mem_n = rms_norm(mem, mem_norm_gain)
    for layer in range(DEPTH):
        g = norm_gains[layer]
        j = layer // 2
        hn = rms_norm(x, g[0])
        if layer % 2 == 0:
            y = mlstm_mixer(hn, ml_w_in[j], ml_b_gate[j], ml_head_gain[j], ml_w_out[j])
        else:
            y = stick_breaking_mixer(hn, sb_w_qkv[j], sb_w_out[j])
        x = x + rms_norm(y, g[1])
        y = memory_cross_attention(rms_norm(x, g[2]), mem_n, xa_w_q[layer], xa_w_kv[layer], xa_w_o[layer])
        x = x + rms_norm(y, g[3])
        y = swiglu_ffn(rms_norm(x, g[4]), ffn_w_gate_up[layer], ffn_w_down[layer])
        x = x + rms_norm(y, g[5])
    return x


DEPTH_2 = 1

CHUNK = 64
Q_BLOCK = 128
EPS = 1e-6

HG_HEADS = 4
HG_DK = 128
HG_DV = 128
HG_WIDTH = HG_HEADS * HG_DK
FOX_HEADS = 8
FOX_DH = 64
FOX_WIDTH = FOX_HEADS * FOX_DH
MEM_HEADS = 4
MEM_DH = 128
MEM_WIDTH = MEM_HEADS * MEM_DH
N_BRANCH = 3
D_FF_2 = 2816
CONV_W = 3

IN_SPLITS = (HG_WIDTH, HG_WIDTH, HG_WIDTH, HG_WIDTH,
             FOX_WIDTH, FOX_WIDTH, FOX_WIDTH, FOX_HEADS,
             MEM_WIDTH, N_BRANCH * D_MODEL)
IN_COLS = 4 * HG_WIDTH + 3 * FOX_WIDTH + FOX_HEADS + MEM_WIDTH + N_BRANCH * D_MODEL


def _split_points():
    pts, acc = [], 0
    for s in IN_SPLITS[:-1]:
        acc += s
        pts.append(acc)
    return pts

def _rmsnorm(x, g):
    xf = x.astype(jnp.float32)
    return xf * lax.rsqrt(jnp.mean(xf * xf, axis=-1, keepdims=True) + EPS) * g.astype(jnp.float32)

def _hgrn2_mixer(q, f_logit, i, g_out, lb, norm_g):
    B, T, _ = q.shape
    n = T // CHUNK

    def heads(z):
        return z.reshape(B, n, CHUNK, HG_HEADS, -1).transpose(1, 0, 3, 2, 4)

    f = lb + (1.0 - lb) * jax.nn.sigmoid(f_logit.astype(jnp.float32))
    qh = heads(jax.nn.silu(q.astype(jnp.float32)))
    kh = heads(1.0 - f)
    ih = heads(i.astype(jnp.float32))
    G = jnp.cumsum(heads(jnp.log(f)), axis=3)
    causal = jnp.tril(jnp.ones((CHUNK, CHUNK), dtype=bool))[:, :, None]

    def step(S, inp):
        qc, kc, ic, Gc = inp
        diff = Gc[:, :, :, None, :] - Gc[:, :, None, :, :]
        decay = jnp.exp(jnp.where(causal, diff, -jnp.inf))
        A = jnp.einsum('bhtc,bhsc,bhtsc->bhts', qc, kc, decay)
        o = (jnp.einsum('bhts,bhsv->bhtv', A, ic)
             + jnp.einsum('bhtc,bhcv->bhtv', qc * jnp.exp(Gc), S))
        G_last = Gc[:, :, -1, :]
        S_new = (S * jnp.exp(G_last)[..., None]
                 + jnp.einsum('bhsc,bhsv->bhcv', kc * jnp.exp(G_last[:, :, None, :] - Gc), ic))
        return S_new, o

    S0 = jnp.zeros((B, HG_HEADS, HG_DK, HG_DV), jnp.float32)
    _, o = lax.scan(step, S0, (qh, kh, ih, G))
    o = o.transpose(1, 0, 3, 2, 4).reshape(B, T, HG_HEADS, HG_DV)
    o = _rmsnorm(o, norm_g).reshape(B, T, HG_WIDTH)
    return o * jax.nn.silu(g_out.astype(jnp.float32))

def _fox_mixer(q, k, v, f_logit, f_bias, q_g, k_g):
    B, T, _ = q.shape
    qh = _rmsnorm(q.reshape(B, T, FOX_HEADS, FOX_DH), q_g).transpose(0, 2, 1, 3)
    kh = _rmsnorm(k.reshape(B, T, FOX_HEADS, FOX_DH), k_g).transpose(0, 2, 1, 3)
    vh = v.astype(jnp.float32).reshape(B, T, FOX_HEADS, FOX_DH).transpose(0, 2, 1, 3)
    log_f = jax.nn.log_sigmoid(f_logit.astype(jnp.float32) + f_bias.astype(jnp.float32))
    Fc = jnp.cumsum(log_f, axis=1).transpose(0, 2, 1)
    scale = FOX_DH ** -0.5
    outs = []
    for blk in range(T // Q_BLOCK):
        lo, hi = blk * Q_BLOCK, (blk + 1) * Q_BLOCK
        s = (jnp.einsum('bhqd,bhkd->bhqk', qh[:, :, lo:hi], kh[:, :, :hi]) * scale
             + Fc[:, :, lo:hi, None] - Fc[:, :, None, :hi])
        mask = (lo + jnp.arange(Q_BLOCK))[:, None] >= jnp.arange(hi)[None, :]
        p = jax.nn.softmax(jnp.where(mask, s, -jnp.inf), axis=-1)
        outs.append(jnp.einsum('bhqk,bhkd->bhqd', p, vh[:, :, :hi]))
    o = jnp.concatenate(outs, axis=2)
    return o.transpose(0, 2, 1, 3).reshape(B, T, FOX_WIDTH)

def _memory_mixer(q, mem_kv, q_g, k_g):
    B, T, _ = q.shape
    M = mem_kv.shape[1]
    qh = _rmsnorm(q.reshape(B, T, MEM_HEADS, MEM_DH), q_g)
    mk, mv = jnp.split(mem_kv, 2, axis=-1)
    kh = _rmsnorm(mk.reshape(B, M, MEM_HEADS, MEM_DH), k_g)
    vh = mv.astype(jnp.float32).reshape(B, M, MEM_HEADS, MEM_DH)
    s = jnp.einsum('bthd,bmhd->bhtm', qh, kh) * (MEM_DH ** -0.5)
    p = jax.nn.softmax(s, axis=-1)
    return jnp.einsum('bhtm,bmhd->bthd', p, vh).reshape(B, T, MEM_WIDTH)

def _conv_glu_ffn(h, w_up, conv_w, conv_b, w_down):
    T = h.shape[1]
    a, v = jnp.split(h @ w_up.astype(jnp.float32), 2, axis=-1)
    ap = jnp.pad(a, ((0, 0), (CONV_W - 1, 0), (0, 0)))
    a = sum(ap[:, j:j + T] * conv_w[j].astype(jnp.float32) for j in range(CONV_W)) + conv_b.astype(jnp.float32)
    return (jax.nn.gelu(a, approximate=False) * v) @ w_down.astype(jnp.float32)

def second_inputs(seed: int = 0) -> dict:
    key = jax.random.key(seed)
    ks = jax.random.split(key, 24)
    f32 = jnp.float32
    L = DEPTH_2

    def nrm(k, shape, fan_in):
        return jax.random.normal(k, shape, f32) * (fan_in ** -0.5)

    def gain(k, shape):
        return 1.0 + 0.02 * jax.random.normal(k, shape, f32)

    return {
        "x": jax.random.normal(ks[0], (BATCH, SEQ, D_MODEL), f32),
        "mem": jax.random.normal(ks[1], (BATCH, N_MEM, D_MODEL), f32),
        "norm_mix_g": gain(ks[2], (L, D_MODEL)),
        "norm_mem_g": gain(ks[3], (L, D_MODEL)),
        "w_in": nrm(ks[4], (L, D_MODEL, IN_COLS), D_MODEL),
        "hgrn_lb_logits": 0.1 * jax.random.normal(ks[5], (L + 1, HG_WIDTH), f32),
        "hgrn_norm_g": gain(ks[6], (L, HG_DV)),
        "fox_f_bias": 1.0 + 0.1 * jax.random.normal(ks[7], (L, FOX_HEADS), f32),
        "fox_q_norm_g": gain(ks[8], (L, FOX_DH)),
        "fox_k_norm_g": gain(ks[9], (L, FOX_DH)),
        "mem_kv_w": nrm(ks[10], (L, D_MODEL, 2 * MEM_WIDTH), D_MODEL),
        "mem_q_norm_g": gain(ks[11], (L, MEM_DH)),
        "mem_k_norm_g": gain(ks[12], (L, MEM_DH)),
        "w_br_hgrn": nrm(ks[13], (L, HG_WIDTH, D_MODEL), HG_WIDTH),
        "w_br_fox": nrm(ks[14], (L, FOX_WIDTH, D_MODEL), FOX_WIDTH),
        "w_br_mem": nrm(ks[15], (L, MEM_WIDTH, D_MODEL), MEM_WIDTH),
        "w_out": nrm(ks[16], (L, D_MODEL, D_MODEL), D_MODEL),
        "norm_ffn_g": gain(ks[17], (L, D_MODEL)),
        "ffn_w_up": nrm(ks[18], (L, D_MODEL, 2 * D_FF_2), D_MODEL),
        "ffn_conv_w": nrm(ks[19], (L, CONV_W, D_FF_2), CONV_W),
        "ffn_conv_b": 0.02 * jax.random.normal(ks[20], (L, D_FF_2), f32),
        "ffn_w_down": nrm(ks[21], (L, D_FF_2, D_MODEL), D_FF_2),
    }

def second_block(x, mem, norm_mix_g, norm_mem_g, w_in, hgrn_lb_logits, hgrn_norm_g, fox_f_bias,
              fox_q_norm_g, fox_k_norm_g, mem_kv_w, mem_q_norm_g, mem_k_norm_g,
              w_br_hgrn, w_br_fox, w_br_mem, w_out, norm_ffn_g, ffn_w_up, ffn_conv_w,
              ffn_conv_b, ffn_w_down):
    B, T, _ = x.shape
    lower_bounds = jnp.cumsum(jax.nn.softmax(hgrn_lb_logits.astype(jnp.float32), axis=0), axis=0)
    pts = _split_points()
    for l in range(DEPTH_2):
        h = _rmsnorm(x, norm_mix_g[l])
        z = h @ w_in[l].astype(jnp.float32)
        (hq, hf, hi, hg, fq, fk, fv, ff, mq, gate_logits) = jnp.split(z, pts, axis=-1)
        y_a = _hgrn2_mixer(hq, hf, hi, hg, lower_bounds[l], hgrn_norm_g[l])
        y_b = _fox_mixer(fq, fk, fv, ff, fox_f_bias[l], fox_q_norm_g[l], fox_k_norm_g[l])
        mem_kv = _rmsnorm(mem, norm_mem_g[l]) @ mem_kv_w[l].astype(jnp.float32)
        y_c = _memory_mixer(mq, mem_kv, mem_q_norm_g[l], mem_k_norm_g[l])
        gates = jax.nn.sigmoid(gate_logits).reshape(B, T, N_BRANCH, D_MODEL)
        merged = (gates[:, :, 0] * (y_a @ w_br_hgrn[l].astype(jnp.float32))
                  + gates[:, :, 1] * (y_b @ w_br_fox[l].astype(jnp.float32))
                  + gates[:, :, 2] * (y_c @ w_br_mem[l].astype(jnp.float32)))
        x = x + (merged @ w_out[l].astype(jnp.float32)).astype(x.dtype)
        h2 = _rmsnorm(x, norm_ffn_g[l])
        x = x + _conv_glu_ffn(h2, ffn_w_up[l], ffn_conv_w[l], ffn_conv_b[l], ffn_w_down[l]).astype(x.dtype)
    return x


def setup_inputs(seed=0):
    out = dict(first_inputs(seed))
    for name, value in second_inputs(seed + 1).items():
        if name != "x":
            out[name + "_2"] = value
    return out


def reference(
    x, mem, mem_norm_gain, norm_gains, ml_w_in, ml_b_gate, ml_head_gain, ml_w_out, sb_w_qkv,
    sb_w_out, xa_w_q, xa_w_kv, xa_w_o, ffn_w_gate_up, ffn_w_down, mem_2, norm_mix_g_2,
    norm_mem_g_2, w_in_2, hgrn_lb_logits_2, hgrn_norm_g_2, fox_f_bias_2, fox_q_norm_g_2,
    fox_k_norm_g_2, mem_kv_w_2, mem_q_norm_g_2, mem_k_norm_g_2, w_br_hgrn_2, w_br_fox_2,
    w_br_mem_2, w_out_2, norm_ffn_g_2, ffn_w_up_2, ffn_conv_w_2, ffn_conv_b_2, ffn_w_down_2,
):
    x = first_block(
        x, mem, mem_norm_gain, norm_gains, ml_w_in, ml_b_gate, ml_head_gain, ml_w_out, sb_w_qkv,
        sb_w_out, xa_w_q, xa_w_kv, xa_w_o, ffn_w_gate_up, ffn_w_down,
    )
    return second_block(
        x, mem_2, norm_mix_g_2, norm_mem_g_2, w_in_2, hgrn_lb_logits_2, hgrn_norm_g_2,
        fox_f_bias_2, fox_q_norm_g_2, fox_k_norm_g_2, mem_kv_w_2, mem_q_norm_g_2,
        mem_k_norm_g_2, w_br_hgrn_2, w_br_fox_2, w_br_mem_2, w_out_2, norm_ffn_g_2, ffn_w_up_2,
        ffn_conv_w_2, ffn_conv_b_2, ffn_w_down_2,
    )


_drawn_inputs = setup_inputs


def setup_inputs(seed=0):
    import zlib

    import numpy as np

    out = dict(_drawn_inputs(seed))
    spreads = {}
    factors = {'ml_head_gain': 2.983,
     'mem_2': 2.677,
     'norm_mix_g_2': 8.0,
     'norm_mem_g_2': 8.0,
     'hgrn_lb_logits_2': 8.0,
     'hgrn_norm_g_2': 8.0,
     'fox_f_bias_2': 8.0,
     'fox_q_norm_g_2': 8.0,
     'fox_k_norm_g_2': 8.0,
     'mem_q_norm_g_2': 8.0,
     'mem_k_norm_g_2': 8.0,
     'norm_ffn_g_2': 8.0,
     'ffn_conv_b_2': 27.442}
    for name, (base, spread) in spreads.items():
        noise = np.random.default_rng([zlib.crc32(name.encode()), seed]).standard_normal(out[name].shape)
        drawn = base * np.exp(spread * noise) if base else spread * noise
        out[name] = __import__('jax').numpy.asarray(drawn.astype(out[name].dtype))
    for name, factor in factors.items():
        out[name] = (out[name] * factor).astype(out[name].dtype)
    return out
```

```python
from contextlib import ExitStack

import concourse.bass as bass
from concourse import mybir

ALU = mybir.AluOpType
ACT = mybir.ActivationFunctionType
AX = mybir.AxisListType
F32 = mybir.dt.float32
BF16 = mybir.dt.bfloat16
F32R = mybir.dt.float32r
U8 = mybir.dt.uint8

EPS = 1e-6
BIG = -1.0e30
D = 1024
NT = 2
FF = 2816
FT = FF // 128
NRAW = 3
NSP = 4

CALLS = {
    "matmul": lambda e, a, k: e.matmul(*a, **k),
    "transpose": lambda e, a, k: e.transpose(*a, **k),
    "activation": lambda e, a, k: e.activation(*a, **k),
    "tensor_copy": lambda e, a, k: e.tensor_copy(*a, **k),
    "tensor_tensor": lambda e, a, k: e.tensor_tensor(*a, **k),
    "tensor_scalar": lambda e, a, k: e.tensor_scalar(*a, **k),
    "scalar_tensor_tensor": lambda e, a, k: e.scalar_tensor_tensor(*a, **k),
    "tensor_tensor_scan": lambda e, a, k: e.tensor_tensor_scan(*a, **k),
    "tensor_reduce": lambda e, a, k: e.tensor_reduce(*a, **k),
    "copy_predicated": lambda e, a, k: e.copy_predicated(*a, **k),
    "reciprocal": lambda e, a, k: e.reciprocal(*a, **k),
    "memset": lambda e, a, k: e.memset(*a, **k),
    "affine_select": lambda e, a, k: e.affine_select(*a, **k),
    "dma_start": lambda e, a, k: e.dma_start(*a, **k),
}


class Queue:

    def __init__(self, sem):
        self.sem = sem
        self.count = 0
        self.items = []

    def put(self, name, args, kw, waits, inc=None, by=1):
        sem = self.sem if inc is None else inc
        self.items.append([name, args, kw, waits, sem, by])

    def hold(self):
        self.items.append([None, (), {}, [], None, 0])
        return self.items[-1]

    def run(self, eng):
        passed = {}
        for name, args, kw, waits, sem, by in self.items:
            for s, v in waits:
                if passed.get(s.name, 0) < v:
                    eng.wait_ge(s, v)
                    passed[s.name] = v
            if name is None:
                continue
            ins = CALLS[name](eng, args, kw)
            if by:
                ins.then_inc(sem, by)


def flat(w):
    if w is None:
        return []
    if isinstance(w, tuple):
        return [w]
    out = []
    for x in w:
        out += flat(x)
    return out


class Tiles:

    def __init__(self, tiles):
        self.tiles = tiles

    def __getitem__(self, i):
        return self.tiles[i[1]][:, i[2]]


class Split:

    def __init__(self, h, l, toks):
        self.h, self.l, self.toks = h, l, toks


def build_program(nc, I, out):
    ctx = ExitStack()
    with ctx:
        def sb(name, shape, dt=F32):
            return ctx.enter_context(nc.sbuf_tensor(name, shape, dt))

        def sem(name):
            return ctx.enter_context(nc.semaphore(name))

        pe, act, dve, pool, sp = (Queue(sem("s_" + n)) for n in ("pe", "act", "dve", "pool", "sp"))

        def push(q, name, args, kw, w, inc=True):
            q.put(name, args, kw, flat(w), by=1 if inc else 0)
            if inc:
                q.count += 1
            return (q.sem, q.count)

        def T(*a, w=None, inc=False, **k):
            return push(pe, "matmul", a, k, w, inc)

        def TR(*a, w=None, inc=False, **k):
            return push(pe, "transpose", a, k, w, inc)

        def A(o, i, f, w=None, **k):
            return push(act, "activation", (o, i, f), k, w)

        def V(name, *a, w=None, **k):
            return push(dve, name, a, k, w)

        def G(name, *a, w=None, **k):
            return push(pool, name, a, k, w)

        def pe_now():
            return (pe.sem, pe.count)

        nd = [0]

        def load(q, dst, src, w=None):
            s = sem(f"s_ld{nd[0]}")
            nd[0] += 1
            q.put("dma_start", (dst, src), {}, flat(w), inc=s, by=16)
            return (s, 16)

        ps = ctx.enter_context(nc.psum_tensor("ps", [128, 8, 512], F32))
        raw = sb("raw", [128, NRAW, 2048])
        whi = sb("whi", [128, NSP, 1024], F32R)
        wlo = sb("wlo", [128, NSP, 1024], F32R)
        xr = sb("xr", [128, NT, D])
        xn = sb("xn", [128, NT, D])
        RR = sb("RR", [128, 11264], F32R)
        Kx = sb("Kx", [128, 8, 256])
        Vx = sb("Vx", [128, NT, D])
        grow = sb("grow", [128, 4, D])
        ident = sb("ident", [128, 128])
        identb = sb("identb", [128, 128], BF16)
        mInc = sb("mInc", [128, 128], BF16)
        mStr = sb("mStr", [128, 128], BF16)
        mRow = sb("mRow", [128, 128], BF16)
        triN = sb("triN", [128, 128])
        onesN = sb("onesN", [128, 128])
        lvl = sb("lvl", [128, 8, 128], U8)
        onesf = sb("onesf", [128, 256])
        gcol = sb("gcol", [128, 240])
        mhalf = sb("mhalf", [128, 8])
        st = sb("st", [128, 600])
        gb = sb("gb", [128, 4])
        fcr = sb("fcr", [8, 256])
        ar = sb("ar", [128, 13056])

        def rr(off, k):
            return RR[:, off:off + 256 * k].rearrange("p (k t) -> p k t", t=256)

        XTh, XTl, memTh, memTl = rr(0, 8), rr(2048, 8), rr(4096, 8), rr(6144, 8)
        nst = [0]

        def stat(n):
            o = nst[0]
            nst[0] += n
            return st[:, o:o + n]

        def reg(off, n):
            return ar[:, off:off + n]

        bfree = [[] for _ in range(8)]

        x2 = I["x"].rearrange("o (t p) d -> p (o t) d", p=128)
        m1 = I["mem"].rearrange("o (t p) d -> p (o t) d", p=128)
        m2 = I["mem_2"].rearrange("o (t p) d -> p (o t) d", p=128)
        grows = reg(12288, 384).rearrange("p (n c) -> p n c", n=3)
        l_x = [load(sp, xr[:, t, :], x2[:, t, :]) for t in range(NT)]
        l_g1 = load(act, grows[0:96, 0, :], I["norm_gains"].rearrange("l i (k p) -> (l i k) p", p=128))
        l_gb = [load(act, gb[0:4, 0:1], I["ml_b_gate"][:, 0:4].rearrange("o p -> p o")),
                load(act, gb[0:4, 1:2], I["ml_b_gate"][:, 4:8].rearrange("o p -> p o"))]
        mem_tm = reg(10240, 2048).rearrange("p (t d) -> p t d", t=2)
        l_mem, l_g2, l_g3 = [], [], []

        def late_loads():
            l_mem.extend(load(sp, mem_tm[:, t, :], m1[:, t, :]) for t in range(NT))
            row = 0
            for nm in ("mem_norm_gain", "ml_head_gain", "norm_mix_g_2", "norm_mem_g_2", "norm_ffn_g_2"):
                v = I[nm] if nm == "mem_norm_gain" else I[nm].rearrange("o d -> (o d)")
                l_g2.append(load(pool, grows[row:row + 8, 1, :], v.rearrange("(k p) -> k p", p=128)))
                row += 8
            l_g2.append(load(pool, grows[40:48, 1, :], I["hgrn_lb_logits_2"].rearrange("l (k p) -> (l k) p", p=128)))
            l_g2.append(load(pool, grows[48:49, 1, :], I["hgrn_norm_g_2"]))
            l_g2.append(load(pool, grows[49:50, 1, :], I["mem_q_norm_g_2"]))
            l_g2.append(load(pool, grows[50:51, 1, :], I["mem_k_norm_g_2"]))
            for i, nm in enumerate(("fox_q_norm_g_2", "fox_k_norm_g_2")):
                for h in range(2):
                    l_g2.append(load(pool, grows[51 + i:52 + i, 1, 64 * h:64 * h + 64], I[nm]))
            l_g3.append(load(pool, grows[0:66, 2, :], I["ffn_conv_w_2"].rearrange("o j (k p) -> (o j k) p", p=128)))
            l_g3.append(load(pool, grows[66:88, 2, :], I["ffn_conv_b_2"].rearrange("o (k p) -> (o k) p", p=128)))
            l_gb.append(load(pool, gb[0:8, 2:3], I["fox_f_bias_2"].rearrange("o p -> p o")))
            for i in range(4):
                rows_at[i] = load_row(i)

        def load_row(i, w=None):
            return load(pool, grow[:, i % 4, :],
                        I["norm_gains"][i // 3, 2 * (i % 3) + 1, :].partition_broadcast(128), w)

        c0 = [G("memset", ident[:, :], 0.0), G("memset", identb[:, :], 0.0), G("memset", mhalf[:, :], -0.5)]
        c_half = c0[2]
        c_id = G("affine_select", ident[:, :], ident[:, :], [[-1, 128]], ALU.not_equal, 1.0, w=c0[0],
                 base=0, channel_multiplier=1)

        def constants():
            c_idb = G("affine_select", identb[:, :], identb[:, :], [[-1, 128]], ALU.not_equal, 1.0, w=c0[1],
                      base=0, channel_multiplier=1)
            c_ms = []
            for m, cm, step, base in ((mInc, -1, 1, 0), (mStr, -1, 1, -1), (mRow, 1, -1, 0)):
                z = G("memset", m[:, :], 0.0)
                c_ms.append(G("affine_select", m[:, :], m[:, :], [[step, 128]], ALU.is_ge, BIG, w=z,
                              base=base, channel_multiplier=cm))
            z = [G("memset", triN[:, :], -1.0), G("memset", onesN[:, :], -1.0), G("memset", onesf[:, :], 1.0)]
            c_ones = z[1:]
            c_tri = G("affine_select", triN[:, :], triN[:, :], [[-1, 128]], ALU.is_ge, 0.0, w=z[0],
                      base=0, channel_multiplier=1)
            lf = Kx[:, 0:4, :].rearrange("p a (i t) -> p (a i) t", t=128)
            z = G("memset", lf, 0.0)
            t = [z]
            for i in range(7):
                L = 1 << i
                nb = 64 // L
                v = lf[:, i, :].rearrange("p (b h l) -> p b h l", h=2, l=L)[:, :, 1, :]
                z1 = G("memset", v, 1.0, w=z)
                z2 = G("affine_select", v, v, [[-2 * L, nb], [0, L]], ALU.is_ge, 0.0, w=z1, base=0, channel_multiplier=1)
                t.append(G("affine_select", v, v, [[2 * L, nb], [0, L]], ALU.is_ge, 0.0, w=z2, base=L - 1,
                           channel_multiplier=-1))
            t.append(G("affine_select", lf[:, 7, :], lf[:, 7, :], [[-1, 128]], ALU.not_equal, 1.0, w=z,
                       base=0, channel_multiplier=1))
            c_lvl = G("tensor_copy", lvl[:, :, :], lf, w=t)
            return c_idb, c_ms, c_ones, c_tri, c_lvl

        gt = [None] * 3

        def gain_columns(i):
            n, l, o = ((96, l_g1, 0), (53, l_g2, 96), (88, l_g3, 149))[i]
            t = TR(ps[:, 6, 0:n], grows[0:n, i, :], ident[0:n, 0:n], w=[l, c_id, bfree[6]], inc=True)
            gt[i] = V("tensor_copy", gcol[:, o:o + n], ps[:, 6, 0:n], w=t)
            bfree[6] = [gt[i]]

        def gain1(l, i):
            return gcol[:, l * 48 + i * 8:l * 48 + i * 8 + 8], gt[0]

        def gain2(r, n=8):
            return gcol[:, 96 + r:96 + r + n], gt[1]

        s_raw = [sem(f"s_w{i}") for i in range(NRAW)]
        n_raw = [0] * NRAW
        raw_free = [None] * NRAW
        s_hi, s_lo = sem("s_hi"), sem("s_lo")
        nchunk, npiece = [0], [0]
        piece_free = {}
        place = {}

        def request(parts, cut):
            r = nchunk[0] % NRAW
            nchunk[0] += 1
            cols = sum(p.shape[1] for p in parts)
            kt = parts[0].shape[0] // 128
            view = raw[:, r, 0:kt * cols].rearrange("p (k c) -> p k c", c=cols)
            c = 0
            for p in parts:
                sp.put("dma_start", (view[:, :, c:c + p.shape[1]], p.rearrange("(k p) c -> p k c", p=128)), {},
                       flat(raw_free[r]), inc=s_raw[r], by=16)
                c += p.shape[1]
                n_raw[r] += 16
            ld = (s_raw[r], n_raw[r])
            if kt * cols <= 1024:
                views = [view]
            elif cut == "k":
                views = [view[:, 0:kt // 2, :], view[:, kt // 2:kt, :]]
            else:
                views = [view[:, :, 0:cols // 2], view[:, :, cols // 2:cols]]
            res = []
            for v in views:
                n = npiece[0]
                npiece[0] += 1
                k, c = v.shape[1], v.shape[2]
                h = whi[:, n % NSP, 0:k * c].rearrange("p (k c) -> p k c", c=c)
                l = wlo[:, n % NSP, 0:k * c].rearrange("p (k c) -> p k c", c=c)
                while n not in place:
                    hold(later.pop(0))
                a, d = place.pop(n)
                a[:] = ["activation", (h, v, ACT.Copy), {}, flat([ld, piece_free.get(n - NSP)]), s_hi, 1]
                d[:] = ["tensor_tensor", (l, v, h.bitcast(F32), ALU.subtract), {},
                        flat([(s_hi, n + 1), piece_free.get(n - NSP)]), s_lo, 1]
                res.append((n, h, l, (s_lo, n + 1)))
            raw_free[r] = (s_lo, npiece[0])
            return res

        def hold(n):
            place[n] = (act.hold(), dve.hold())

        later = []
        defer = [False]

        def release(n, tok):
            piece_free[n] = tok
            if defer[0]:
                later.append(n + NSP)
            else:
                hold(n + NSP)

        def settle(n):
            while later and n:
                hold(later.pop(0))
                n -= 1
            defer[0] = False

        bank_n = [0]

        ring = [0, 1, 2, 3]

        def nextbank():
            bank_n[0] += 1
            return ring[bank_n[0] % len(ring)]

        def fm_piece(o, piece, X, w=None):
            n, h, l, ld = piece
            kt = h.shape[1]
            for k in range(kt):
                T(o, h[:, k, :], X.h[:, k, :], start=k == 0, stop=False, w=[ld, X.toks[k], w])
                T(o, h[:, k, :], X.l[:, k, :], start=False, stop=False)
                t = T(o, l[:, k, :], X.h[:, k, :], start=False, stop=k == kt - 1, inc=k == kt - 1)
            release(n, t)
            return t

        def fm_chunk(parts, X, bank=None):
            b = nextbank() if bank is None else bank
            for i, p in enumerate(request(parts, "c")):
                t = fm_piece(ps[:, b, 256 * i:256 * i + 256], p, X, bfree[b])
            return b, t

        def tm_pieces(pieces, X, k0, K, banks, half=None):
            toks = []
            for t in range(NT):
                r = slice(128 * t, 128 * t + 128)
                for i, (n, h, l, ld) in enumerate(pieces):
                    kt = h.shape[1]
                    for b, c in banks[t]:
                        for k in range(kt):
                            g = k0 + kt * i + k
                            first, last = g == 0, g == K - 1
                            o = ps[:, b, 0:512]
                            T(o, X.h[:, g, r], h[:, k, c:c + 512], start=first, stop=False,
                              w=[ld, X.toks[g], bfree[b] if first else None])
                            T(o, X.h[:, g, r], l[:, k, c:c + 512], start=False, stop=False)
                            m = T(o, X.l[:, g, r], h[:, k, c:c + 512], start=False, stop=last, inc=k == kt - 1)
                    if t == NT - 1:
                        release(n, m)
                toks.append(m)
            return toks

        def tm_steps(W, c0, X, banks=None):
            K = W.shape[0] // 128
            banks = banks or (nextbank(), nextbank())
            toks = None
            for k in range(0, K, 4):
                pieces = request([W[128 * k:128 * k + 512, c0:c0 + 512]], "k")
                toks = tm_pieces(pieces, X, k, K, [[(banks[0], 0)], [(banks[1], 0)]])
                yield banks, toks if k + 4 >= K else None

        def tm_block(W, c0, X, banks=None):
            for got in tm_steps(W, c0, X, banks):
                pass
            return got

        def rstd(ss, n, cnt, w):
            m, r = stat(n), stat(n)
            t = G("tensor_scalar", m, ss, 1.0 / cnt, EPS, ALU.mult, ALU.add, w=w)
            return r, G("tensor_tensor", r, m, mhalf[:, 0:n], ALU.pow, w=[t, c_half])

        xn_free = []

        def put(q, o, i, w, scale=None):
            if q == "act":
                return A(o, i, ACT.Copy, w=w, **({} if scale is None else {"scale": scale}))
            if scale is None:
                return V("tensor_copy", o, i, w=w)
            return V("tensor_scalar", o, i, scale, None, ALU.mult, w=w)

        def put_split(h, l, i, w, wfree, gain=None):
            a = put("act", h, i, [w, wfree], gain)
            if gain is None:
                return V("tensor_tensor", l, i, h.bitcast(F32), ALU.subtract, w=[a, wfree])
            return V("scalar_tensor_tensor", l, i, gain, h.bitcast(F32), ALU.mult, ALU.subtract, w=[a, wfree])

        def turn(src, nk, toks, h, l, gains, dst_free, banks=(4, 5, 0, 1)):
            nb = len(banks)
            last = [None] * nk
            for t in range(NT):
                for k in range(nk):
                    b, o = banks[k % nb], 256 * (k // nb)
                    last[k] = TR(ps[:, b, o + 128 * t:o + 128 * t + 128], src[:, t, 128 * k:128 * k + 128], ident[:, :],
                                 w=[toks[t], c_id, bfree[b] if t == 0 and k < nb else None], inc=t == 1)
            done = []
            for k in range(nk):
                b, o = banks[k % nb], 256 * (k // nb)
                g, gw = gains(k)
                i = ps[:, b, o:o + 256]
                w = [last[k], last[k + nb] if k + nb < nk else None, gw, done[k - nb] if k >= nb else None]
                if l is None:
                    e = put("act" if k % nb % 2 else "dve", h[:, k, :], i, [w, dst_free], g)
                else:
                    e = put_split(h[:, k, :], l[:, k, :], i, w, dst_free, g)
                    if k == 1:
                        settle(1)
                done.append(e)
                bfree[b] = [e]
            return done, last[-1]

        def normed(x, xt, o, free):
            toks = []
            for t in range(NT):
                ss = stat(1)
                a = A(o[:, t, :], x[:, t, :], ACT.Square, accum_out=ss, w=[xt[t], free])
                r, rt = rstd(ss, 1, D, a)
                toks.append(V("tensor_scalar", o[:, t, :], x[:, t, :], r, None, ALU.mult, w=[rt, xt[t], a]))
            return toks

        def norm_T(x, xt, gain, h, l, dst_free, before=0, after=0, banks=(4, 5, 0, 1)):
            toks = normed(x, xt, xn, xn_free)
            defer[0] = before > 0 and after == 0
            fill(before, False)
            g, gw = gain
            got, tr = turn(xn, 8, toks, h, l, lambda k: (g[:, k:k + 1], gw), dst_free, banks)
            xn_free[:] = [tr]
            settle(NSP)
            fill(after)
            return Split(h, l, got)

        def turn_steps(tag, src, toks, gain, h, l, dst_free, banks=(6, 7)):
            g, gw = gain
            done = []
            for k0 in (0, 4):
                d, tr = turn(src[:, :, 128 * k0:128 * k0 + 512], 4, toks, h[:, k0:k0 + 4, :], l[:, k0:k0 + 4, :],
                             lambda k: (g[:, k0 + k:k0 + k + 1], gw), dst_free, banks)
                done += d
                if k0 == 4:
                    ready[tag] = done
                yield False

        rows_at = {}

        def post_add(toks, gi, xt):
            new = []
            for t in range(NT):
                y = ps[:, 2 * t:2 * t + 2, :]
                ss = stat(1)
                yv = xn[:, t, :].rearrange("p (h c) -> p h c", h=2)
                a = A(yv, y, ACT.Square, accum_out=ss, w=[toks[t], xn_free])
                r, rt = rstd(ss, 1, D, a)
                m = V("tensor_tensor", yv, y, grow[:, gi % 4, :].rearrange("p (h c) -> p h c", h=2), ALU.mult,
                      w=[rows_at[gi], a])
                bfree[2 * t] = bfree[2 * t + 1] = [m]
                new.append(V("scalar_tensor_tensor", xr[:, t, :], xn[:, t, :], r, xr[:, t, :], ALU.mult, ALU.add,
                             w=[rt, m, xt[t]]))
            xn_free[:] = new
            if gi + 4 < 6:
                rows_at[gi + 4] = load_row(gi + 4, m)
            return new, m

        def out_steps(W, X):
            for k in range(0, 8, 4):
                for h in range(2):
                    pieces = request([W[128 * k:128 * k + 512, 512 * h:512 * h + 512]], "k")
                    yield tm_pieces(pieces, X, k, 8, [[(h, 0)], [(2 + h, 0)]])

        def out_proj(W, X):
            for toks in out_steps(W, X):
                pass
            return toks

        def proj_fm(W, c0, n, X, dst, dst_free, scale=None):
            res = []
            for c in range(0, n, 256):
                b, t = fm_chunk([W[:, c0 + c:c0 + c + 256]], X)
                j = c // 128
                e = put("act" if j % 4 else "dve", dst[:, j:j + 2, :], ps[:, b, :].rearrange("p (a c) -> p a c", a=2),
                        [t, dst_free], scale)
                bfree[b] = [e]
                res += [e, e]
            return res

        def proj_tm(W, c0, n, X, dst, dst_free):
            res = []
            for c in range(0, n, 512):
                pr, toks = tm_block(W, c0 + c, X)
                for t in range(NT):
                    e = put("act" if t == 0 else "dve", dst(t, c), ps[:, pr[t], :], [toks[t], dst_free])
                    bfree[pr[t]] = [e]
                    res.append(e)
            return res

        def gate_rows(W, c0, m, n, X):
            b = nextbank()
            i, h, l, ld = request([W[:, c0:c0 + m * n]], "c")[0]
            for j in range(n):
                o, c = ps[0:m, b, 256 * j:256 * j + 256], slice(m * j, m * j + m)
                for k in range(8):
                    T(o, h[:, k, c], X.h[:, k, :], start=k == 0, stop=False, w=[ld, X.toks[k], bfree[b]])
                    T(o, h[:, k, c], X.l[:, k, :], start=False, stop=False)
                    t = T(o, l[:, k, c], X.h[:, k, :], start=False, stop=k == 7, inc=k == 7)
            release(i, t)
            return b, t

        def feed_forward(Wup, Wdown, X, hidden, free):
            Hr = [rr(8192 + 1024 * i, 4) for i in range(3)]
            made = {}
            used = {}

            def down(j):
                h = Hr[j % 3]
                S = Split(h[:, 0:2, :], h[:, 2:4, :], made[j])
                for i, (n, wh, wl, ld) in enumerate(request([Wdown[256 * j:256 * j + 256, :]], "k")):
                    toks = []
                    for t in range(NT):
                        r = slice(128 * t, 128 * t + 128)
                        for half in range(2):
                            b, c = 2 * t + half, slice(512 * half, 512 * half + 512)
                            first, last = j == 0 and i == 0, j == FT // 2 - 1 and i == 1
                            T(ps[:, b, :], S.h[:, i, r], wh[:, 0, c], start=first, stop=False,
                              w=[ld, S.toks, bfree[b] if first else None])
                            T(ps[:, b, :], S.h[:, i, r], wl[:, 0, c], start=False, stop=False)
                            m = T(ps[:, b, :], S.l[:, i, r], wh[:, 0, c], start=False, stop=last, inc=half == 1)
                        toks.append(m)
                    release(n, m)
                used[j] = m
                return toks

            for j in range(FT // 2):
                bg, bu = 4 + 2 * (j % 2), 5 + 2 * (j % 2)
                _, tg = fm_chunk([Wup[:, 256 * j:256 * j + 256]], X, bg)
                _, tu = fm_chunk([Wup[:, FF + 256 * j:FF + 256 * j + 256]], X, bu)
                tmp = reg(512 * (j % 2), 512)
                prod = reg(1024 + 512 * (j % 2), 512)
                e = hidden(j, bg, tg, tmp, [free, made.get(j - 2)])
                p = V("tensor_tensor", prod, ps[:, bu, :], tmp, ALU.mult, w=[tu, e, free, made.get(j - 2)])
                bfree[bu] = [p]
                h = Hr[j % 3]
                made[j] = put_split(h[:, 0:2, :].rearrange("p a t -> p (a t)"), h[:, 2:4, :].rearrange("p a t -> p (a t)"),
                                    prod, p, used.get(j - 3))
                xdone = tu
                if j:
                    down(j - 1)
            return down(FT // 2 - 1), xdone

        fillers = []
        mid = [False]

        def fill(n, whole=True):
            while (n > 0 or (whole and mid[0])) and fillers:
                try:
                    mid[0] = next(fillers[0])
                    n -= 0 if whole and mid[0] else 1
                except StopIteration:
                    fillers.pop(0)

        def drain(tag):
            while tag not in ready:
                fill(1)

        ready = {}

        def evac(dst, free):
            def run(bk, toks):
                es = []
                for t in range(NT):
                    e = put("act" if t else "dve", dst(t), ps[:, bk[t], :], [toks[t], free])
                    bfree[bk[t]] = [e]
                    es.append(e)
                return es
            return run

        def through(dst, f, free):
            def run(bk, toks):
                es = []
                for t in range(NT):
                    e = A(dst(t), ps[:, bk[t], :], f, w=[toks[t], free])
                    bfree[bk[t]] = [e]
                    es.append(e)
                return es
            return run

        def tm_work(tag, W, c0, X, take, banks=None):
            banks = banks and tuple(banks)
            for bk, toks in tm_steps(W, c0, X, banks):
                if toks:
                    ready[tag] = take(bk, toks)
                yield toks is None

        kvb = [6, 7, 6, 7]

        def cross_kv(l, X, kfree, vfree):
            W = I["xa_w_kv"][l]

            def keys(j):
                b, t = fm_chunk([W[:, 256 * j:256 * j + 256]], X, kvb[j % 2])
                e = put("act" if j % 2 else "dve", Kx[:, 2 * j:2 * j + 2, :], ps[:, b, :].rearrange("p (a c) -> p a c", a=2),
                        [t, kfree])
                bfree[b] = [e]
                ready[("K", l, j)] = e

            def values(j):
                return tm_work(("V", l, j), W, 1024 + 512 * j, X, evac(lambda t: Vx[:, t, 512 * j:512 * j + 512], vfree), kvb[2:4])

            for j in range(3):
                keys(j)
                yield False
            for m in values(0):
                yield m
            keys(3)
            yield False
            for m in values(1):
                if not m:
                    ready[("KV", l)] = pe_now()
                yield m

        def memory_attention(nk, qof, kof, ktok, v, vtok, scale, base, free, oh, ol, ofree, otok):
            P = [reg(base + 512 * i, 512).rearrange("p (t m) -> p t m", t=2) for i in range(3)]
            PT = [reg(base + 1536 + 512 * i, 512).rearrange("p (m t) -> p m t", m=2) for i in range(2)]
            q, ex, pt, ptr, pvd = {}, {}, {}, {}, {}

            def scores(h):
                b = 4 + h % 2
                qT, qt = q[h]
                for t in range(NT):
                    for k in range(nk):
                        s = T(ps[:, b, 256 * t:256 * t + 256], qT[:, k, 128 * t:128 * t + 128], kof(h)[:, k, :], start=k == 0,
                              stop=k == nk - 1, w=[qt, ktok(h), bfree[b] if t == 0 else None], inc=k == nk - 1)
                sv = ps[:, b, :].rearrange("p (t m) -> p t m", t=2)
                nm, ns, sm, ri = stat(2), stat(2), stat(2), stat(2)
                m = V("tensor_reduce", nm, sv, AX.X, ALU.max, negate=True, w=s)
                m = V("tensor_scalar", ns, nm, scale, None, ALU.mult, w=m)
                for t in range(NT):
                    e = A(P[h % 3][:, t, :], sv[:, t, :], ACT.Exp, bias=ns[:, t:t + 1], scale=scale,
                          accum_out=sm[:, t:t + 1], w=[m, free, ptr.get(h - 3)])
                bfree[b] = [e]
                r = V("reciprocal", ri, sm, w=e)
                ex[h] = V("tensor_tensor", P[h % 3], P[h % 3], ri.unsqueeze(2).to_broadcast([128, 2, 256]), ALU.mult, w=[r, e])

            def weights(h):
                for m in range(2):
                    for t in range(NT):
                        s = TR(ps[:, 6, 256 * m + 128 * t:256 * m + 128 * t + 128], P[h % 3][:, t, 128 * m:128 * m + 128],
                               ident[:, :], w=[ex[h], bfree[6]], inc=m == 1 and t == 1)
                ptr[h] = s
                pt[h] = put("act", PT[h % 2], ps[:, 6, :].rearrange("p (m t) -> p m t", m=2), [s, free, pvd.get(h - 2)])
                bfree[6] = [pt[h]]

            def values(h):
                for j in range(nk):
                    d = 128 * (h * nk + j)
                    for m in range(2):
                        s = T(ps[:, 7, 256 * j:256 * j + 256], v[:, m, d:d + 128], PT[h % 2][:, m, :], start=m == 0, stop=m == 1,
                              w=[pt[h], vtok(h), bfree[7] if j == 0 else None], inc=m == 1)
                pvd[h] = s
                e = put_split(oh[:, h * nk:h * nk + nk, :].rearrange("p a t -> p (a t)"),
                              ol[:, h * nk:h * nk + nk, :].rearrange("p a t -> p (a t)"), ps[:, 7, 0:256 * nk], s, ofree())
                bfree[7] = [e]
                otok.extend([e] * nk)

            for i in range(4 + 3):
                if i < 4:
                    q[i] = qof(i)
                yield i, 0
                if 1 <= i < 5:
                    scores(i - 1)
                if 2 <= i < 6:
                    weights(i - 2)
                if i >= 3:
                    values(i - 3)
                yield i, 1

        gain_columns(0)
        xt = l_x
        later.extend(range(NSP))
        X = norm_T(xr, xt, gain1(0, 0), XTh, XTl, None)
        c_idb, c_ms, c_ones, c_tri, c_lvl = constants()

        W = I["ml_w_in"][0]
        q3 = reg(0, 1024).rearrange("p (h t) -> p h t", h=4)
        k3 = reg(1024, 1024).rearrange("p (h t) -> p h t", h=4)
        V4 = reg(2048, 2064).rearrange("p (t h d) -> p t h d", t=2, h=4)
        DP = reg(4112, 1536).rearrange("p (h c) -> p h c", h=4)
        og = reg(5648, 2048).rearrange("p (t d) -> p t d", t=2)
        sq = reg(9488, 512)
        rows = reg(7696, 1792).rearrange("p (n t) -> p n t", t=256)
        b, tg = gate_rows(W, 3072, 4, 2, X)
        b15 = stat(2)
        sc15 = V("tensor_scalar", b15[0:4, :], gb[0:4, 0:2], 1.0 / 15.0, None, ALU.mult, w=l_gb)
        ig, fg, spc, av, mv, dv, ng = (rows[0:4, i, :] for i in range(7))
        a1 = A(ig, ps[0:4, b, 0:256], ACT.Tanh, bias=b15[0:4, 0:1], scale=1.0 / 15.0, w=[tg, sc15])
        a2 = A(fg, ps[0:4, b, 256:512], ACT.Tanh, bias=b15[0:4, 1:2], scale=1.0 / 15.0, w=[tg, sc15])
        bfree[b] = [a2]
        a2 = A(fg, fg, ACT.Exp, scale=-15.0, w=a2)
        a2 = A(fg, fg, ACT.Ln, bias=1.0, w=a2)
        s1 = V("tensor_tensor_scan", spc, onesf[0:4, :], fg, 0.0, ALU.mult, ALU.add, w=[a2, c_ones])
        s2 = V("scalar_tensor_tensor", av, ig, 15.0, spc, ALU.mult, ALU.add, w=[a1, s1])
        s3 = V("tensor_tensor_scan", mv, av, av, 0.0, ALU.max, ALU.max, w=s2)
        s4 = V("tensor_tensor", dv, spc, mv, ALU.subtract, w=s3)
        s5 = V("tensor_scalar", ng, mv, -1.0, None, ALU.mult, w=s3)
        qt = proj_fm(W, 0, 512, X, q3, None)
        late_loads()
        kt = proj_fm(W, 512, 512, X, k3, None)
        mem_n = reg(5648, 2048).rearrange("p (t d) -> p t d", t=2)
        mnt = normed(mem_tm, l_mem, mem_n, None)
        fillers.append(turn_steps("M", mem_n, mnt, gain2(0), memTh, memTl, None))
        ptk, ce, emc = [], None, stat(16)

        def decays():
            nonlocal ce
            for t in range(NT):
                TR(ps[:, 4, 8 * t:8 * t + 4], av[:, 128 * t:128 * t + 128], ident[0:4, 0:4], w=[s2, bfree[4]])
                tc = TR(ps[:, 4, 8 * t + 4:8 * t + 8], dv[:, 128 * t:128 * t + 128], ident[0:4, 0:4], w=s4, inc=True)
            acol = stat(16)
            cc = V("tensor_copy", acol, ps[:, 4, 0:16], w=tc)
            bfree[4] = [cc]
            ce = A(emc, acol, ACT.Exp, w=cc)
            for h in range(4):
                bk = 4 + h
                T(ps[:, bk, 0:128], identb[:, :], mInc[:, :], start=True, stop=False, w=[c_idb, c_ms, bfree[bk]],
                  skip_group_check=True)
                T(ps[:, bk, 256:384], identb[:, :], mInc[:, :], start=False, stop=False, skip_group_check=True)
                sel = ident[0:4, h:h + 1].to_broadcast([4, 128])
                T(ps[:, bk, 0:256], sel, ng, start=False, stop=False, w=[s5, c_id], skip_group_check=True)
                m = T(ps[:, bk, 256:384], sel, ng[:, 128:256], start=False, stop=True, inc=True, skip_group_check=True)
                A(DP[:, h, 0:256], ps[:, bk, 0:256], ACT.Exp, bias=acol[:, h:h + 1], w=[m, cc])
                e = A(DP[:, h, 256:384], ps[:, bk, 256:384], ACT.Exp, bias=acol[:, 8 + h:9 + h])
                bfree[bk] = [e]

        def weights():
            for h in range(4):
                bk = 4 + h
                T(ps[:, bk, 0:256], k3[:, h, 0:128], q3[:, h, :], start=True, stop=True, w=[kt[h], qt[h], bfree[bk]])
                m = T(ps[:, bk, 256:384], k3[:, h, 128:256], q3[:, h, 128:256], start=True, stop=True, inc=True)
                e = V("scalar_tensor_tensor", DP[:, h, :], ps[:, bk, 0:384], 128.0 ** -0.5, DP[:, h, :], ALU.mult, ALU.mult,
                      w=[m, bfree[bk]])
                bfree[bk] = [e]
                ptk.append(e)

        vone = G("memset", V4[:, :, :, 256:257], 1.0)
        vt = []
        for c in (0, 512):
            pr, toks = tm_block(W, 1024 + c, X)
            if c:
                weights()
            else:
                decays()
            for t in range(NT):
                e = put("act" if t == 0 else "dve", V4[:, t, c // 256:c // 256 + 2, 0:256],
                        ps[:, pr[t], :].rearrange("p (h c) -> p h c", h=2), toks[t])
                bfree[pr[t]] = [e]
                vt.append(e)
            if not c:
                gain_columns(1)
            fill(1 + c)
        M = Split(memTh, memTl, ready["M"])
        ogt = [[], []]
        for c in (0, 512):
            pr, toks = tm_block(W, 2048 + c, X)
            for t in range(NT):
                e = A(og[:, t, c:c + 512], ps[:, pr[t], :], ACT.Sigmoid, w=[toks[t], M.toks])
                bfree[pr[t]] = [e]
                ogt[t].append(e)
        xt_free = toks[1]
        fillers.append(cross_kv(0, M, c_lvl, None))
        kvb[:] = [0, 1, 2, 3]
        zt = []
        s = None
        for t in range(NT):
            ts = []
            for h in range(4):
                bk = 4 + h
                o = ps[:, bk, 0:257]
                if t == 0:
                    m = T(o, DP[:, h, 0:128], V4[:, 0, h, 0:257], start=True, stop=True, w=[ptk[h], vt, vone, bfree[bk]],
                          inc=True)
                else:
                    T(o, DP[:, h, 128:256], V4[:, 0, h, 0:257], start=True, stop=False, w=bfree[bk])
                    m = T(o, DP[:, h, 256:384], V4[:, 1, h, 0:257], start=False, stop=True, inc=True)
                ts.append(m)
            dn, rd, ss = stat(4), stat(4), stat(4)
            den = ps[:, 4:8, 256:257].rearrange("p h o -> p (h o)")
            dm = stat(4)
            e = V("tensor_copy", dn, den, w=ts)
            e = V("scalar_tensor_tensor", dm, dn, -1.0, emc[:, 8 * t + 4:8 * t + 8], ALU.mult, ALU.max, w=[e, ce])
            e = V("tensor_tensor", dn, dn, dm, ALU.max, w=e)
            e = V("reciprocal", rd, dn, w=e)
            hs = xn[:, t, :].rearrange("p (h d) -> p h d", h=4)
            e = V("tensor_tensor", hs, ps[:, 4:8, 0:256], rd.unsqueeze(2).to_broadcast([128, 4, 256]), ALU.mult,
                  w=[e, xn_free])
            for bk in range(4, 8):
                bfree[bk] = [e]
            for h in range(4):
                s = A(sq[:, 0:256], hs[:, h, :], ACT.Square, accum_out=ss[:, h:h + 1], w=[e, s])
            r, rt = rstd(ss, 4, 256, s)
            for h in range(4):
                e = V("scalar_tensor_tensor", hs[:, h, :], hs[:, h, :], r[:, h:h + 1], og[:, t, 256 * h:256 * h + 256],
                      ALU.mult, ALU.mult, w=[rt, ogt[t]])
            zt.append(e)
            fill(1 + t)
        kvb[:] = [6, 7, 6, 7]
        g, gw = gain2(8)
        oTt, tr = turn(xn, 8, zt, XTh, XTl, lambda k: (g[:, k:k + 1], gw), xt_free)
        xn_free[:] = [tr]
        fill(1)
        yt = out_proj(I["ml_w_out"][0], Split(XTh, XTl, oTt))
        xt_free = pe_now()
        xt, _ = post_add(yt, 0, xt)
        ar_free = [yt[1], zt, ogt]

        def cross_attention(l, xt, free, xt_free, before, after, between=0):
            X = norm_T(xr, xt, gain1(l, 2), XTh, XTl, xt_free, before, after)
            drain(("KV", l))
            q = [reg(512 * i, 512).rearrange("p (k t) -> p k t", k=2) for i in range(3)]
            qread = {}
            W = I["xa_w_q"][l]

            def qof(h):
                if h:
                    qread[h - 1] = pe_now()
                b, t = fm_chunk([W[:, 256 * h:256 * h + 256]], X)
                e = put("dve", q[h % 3], ps[:, b, :].rearrange("p (k c) -> p k c", k=2), [t, free, qread.get(h - 1)])
                bfree[b] = [e]
                qread["all"] = t
                return q[h % 3], e

            O = Split(XTh, XTl, [])
            y = out_steps(I["xa_w_o"][l], O)
            for i, stage in memory_attention(2, qof, lambda h: Kx[:, 2 * h:2 * h + 2, :], lambda h: ready[("K", l, h)], Vx,
                                             lambda h: ready[("V", l, h // 2)], 256.0 ** -0.5, 1536, free, XTh, XTl,
                                             lambda: qread["all"], O.toks):
                if (i, stage) in ((4, 1), (5, 1)):
                    next(y)
                if (i, stage) in ((0, 1), (1, 1)):
                    fill(between)
            pv = pe_now()
            for yt in y:
                pass
            xt, m = post_add(yt, 3 * l + 1, xt)
            return xt, pe_now(), pv

        def swiglu(j, b, tok, tmp, w):
            e = A(tmp, ps[:, b, :], ACT.Silu, w=[tok, w])
            bfree[b] = [e]
            return e

        def ffn(l, xt, free, xt_free, before, after):
            X = norm_T(xr, xt, gain1(l, 4), XTh, XTl, xt_free, before, after)
            yt, xdone = feed_forward(I["ffn_w_gate_up"][l], I["ffn_w_down"][l], X, swiglu, free)
            xt, m = post_add(yt, 3 * l + 2, xt)
            return xt, pe_now(), xdone, m

        xt, xa_done, pv = cross_attention(0, xt, ar_free, xt_free, 2, 3)
        fillers.append(cross_kv(1, M, pv, pv))
        xt, ff_done, up_done, _ = ffn(0, xt, [xa_done], xa_done, 2, 1)

        X = norm_T(xr, xt, gain1(1, 0), XTh, XTl, up_done, 2, 0)
        W = I["sb_w_qkv"][0]
        qT = reg(0, 2048).rearrange("p (k t) -> p k t", k=8)
        kT = reg(2048, 2048).rearrange("p (k t) -> p k t", k=8)
        Vs = reg(4096, 2048).rearrange("p (t d) -> p t d", t=2)
        Sp = [reg(6144 + 768 * i, 768).rearrange("p (h c) -> p h c", h=2) for i in range(3)]
        Aw = [reg(8448 + 768 * i, 768).rearrange("p (h c) -> p h c", h=2) for i in range(2)]
        qt, kt, vt, sptok, trit, atok, pvt, oT = {}, {}, {}, {}, {}, {}, {}, []
        Or = [rr(8192 + 1024 * i, 4) for i in range(3)]
        Oh = Tiles([Or[i // 2][:, i % 2, :] for i in range(6)] + [XTh[:, 6, :], XTh[:, 7, :]])
        Ol = Tiles([Or[i // 2][:, 2 + i % 2, :] for i in range(6)] + [XTl[:, 6, :], XTl[:, 7, :]])
        Oh2 = [r[:, 0:2, :] for r in Or] + [XTh[:, 6:8, :]]
        Ol2 = [r[:, 2:4, :] for r in Or] + [XTl[:, 6:8, :]]

        def sb_fm(c, dst, tok, c0, q, scale):
            b, t = fm_chunk([W[:, c0 + 256 * c:c0 + 256 * c + 256]], X)
            e = put(q, dst[:, 2 * c:2 * c + 2, :], ps[:, b, :].rearrange("p (a c) -> p a c", a=2), [t, ff_done], scale)
            bfree[b] = [e]
            tok[2 * c] = tok[2 * c + 1] = e

        def sb_q(c):
            sb_fm(c, qT, qt, 0, "act", 0.125)

        def sb_k(c):
            sb_fm(c, kT, kt, 1024, "dve", None)

        def sb_v(j):
            take = evac(lambda t: Vs[:, t, 512 * j:512 * j + 512], ff_done)
            bk, toks = tm_block(W, 2048 + 512 * j, X)
            vt[j] = take(bk, toks)

        def sb_scores(p):
            bk = 4 + 2 * (p % 2)
            for h in range(2):
                o = ps[:, bk + h, :]
                r = slice(64 * h, 64 * h + 64)
                T(o[:, 0:128], identb[:, :], mStr[:, :], start=True, stop=False, w=[c_idb, c_ms, bfree[bk + h]],
                  skip_group_check=True)
                T(o[:, 256:384], identb[:, :], mStr[:, :], start=False, stop=False, skip_group_check=True)
                T(o[:, 0:256], kT[r, p, 0:128], qT[r, p, :], start=False, stop=False, w=[qt[p], kt[p]],
                  skip_group_check=True)
                m = T(o[:, 256:384], kT[r, p, 128:256], qT[r, p, 128:256], start=False, stop=False,
                      skip_group_check=True, inc=h == 1)
            z = ps[:, bk:bk + 2, 0:384]
            s = Sp[p % 3]
            a = A(s, z, ACT.Abs, w=[m, trit.get(p - 3), ff_done])
            a = A(s, s, ACT.Exp, scale=-1.0, w=a)
            a = A(s, s, ACT.Ln, bias=1.0, w=a)
            sptok[p] = V("scalar_tensor_tensor", s, z, 0.0, s, ALU.max, ALU.add, w=a)

        def sb_weights(p):
            bk = 4 + 2 * (p % 2)
            for h in range(2):
                o = ps[:, bk + h, :]
                s = Sp[p % 3][:, h, :]
                T(o[:, 0:256], triN[:, :], s[:, 0:256], start=False, stop=False, w=[sptok[p], c_tri, c_ones],
                  skip_group_check=True)
                T(o[:, 128:256], onesN[:, :], s[:, 256:384], start=False, stop=False, skip_group_check=True)
                m = T(o[:, 256:384], triN[:, :], s[:, 256:384], start=False, stop=True, skip_group_check=True,
                      inc=h == 1)
            trit[p] = m
            atok[p] = A(Aw[p % 2], ps[:, bk:bk + 2, 0:384], ACT.Exp, w=[m, pvt.get(p - 2), ff_done])
            bfree[bk] = bfree[bk + 1] = [atok[p]]

        def sb_values(p):
            bk, c = 3, 256 * (p % 2)
            for h in range(2):
                o = ps[64 * h:64 * h + 64, bk, :]
                d = 128 * p + 64 * h
                T(o[:, c:c + 256], Vs[:, 0, d:d + 64], Aw[p % 2][:, h, 0:256], start=True, stop=False,
                  w=[atok[p], vt[p // 4], bfree[bk] if p % 2 == 0 else None], skip_group_check=True)
                m = T(o[:, c + 128:c + 256], Vs[:, 1, d:d + 64], Aw[p % 2][:, h, 256:384], start=False, stop=True,
                      skip_group_check=True, inc=h == 1)
            pvt[p] = m
            if p % 2:
                e = put_split(Oh2[p // 2], Ol2[p // 2], ps[:, bk, :].rearrange("p (a c) -> p a c", a=2), m, [ff_done, sbx])
                bfree[bk] = [e]
                oT.extend([e, e])

        y = out_steps(I["sb_w_out"][0], Split(Oh, Ol, oT))
        dense = {0: [(sb_q, 0), (sb_k, 0), (sb_q, 1)], 1: [(sb_k, 1), (sb_v, 0)], 2: [(sb_q, 2)], 3: [(sb_k, 2), (sb_q, 3)],
                 4: [(sb_v, 1)], 5: [(sb_k, 3)]}
        ring[:] = [0, 1, 2]
        kvb[:] = [0, 1, 0, 1]
        sbx = None
        for i in range(8 + 2):
            for f, a in dense.get(i, []):
                f(a)
            if i == 6:
                sbx = pe_now()
                fill(1)
            if i == 7:
                next(y)
            if i < 8:
                sb_scores(i)
            if 1 <= i < 9:
                sb_weights(i - 1)
            if i >= 2:
                sb_values(i - 2)
        ring[:] = [0, 1, 2, 3]
        kvb[:] = [6, 7, 6, 7]
        for yt in y:
            pass
        sb_done = pe_now()
        xt, _ = post_add(yt, 3, xt)
        l_mem2 = [load(pool, mem_tm[:, t, :], m2[:, t, :], w=M.toks) for t in range(NT)]
        mem_n = reg(6144, 2048).rearrange("p (t d) -> p t d", t=2)

        mnt = []

        def mem2_norm():
            mnt.extend(normed(mem_tm, l_mem2, mem_n, sb_done))
            yield False

        def mem2_turn():
            for m in turn_steps("M2", mem_n, mnt, gain2(24), memTh, memTl, ready[("KV", 1)]):
                yield m

        fillers.insert(0, mem2_norm())
        fillers.append(mem2_turn())
        xt, xa_done, pv = cross_attention(1, xt, [sb_done], sb_done, 3, 0, 1)
        gain_columns(2)
        drain("M2")
        M2 = Split(memTh, memTl, ready["M2"])
        mk = Vx[:, 0, :].rearrange("p (t d) -> p t d", t=2)
        mv = Vx[:, 1, :].rearrange("p (t d) -> p t d", t=2)
        Wm = I["mem_kv_w_2"][0]
        fillers.append(tm_work("mk", Wm, 0, M2, evac(lambda t: mk[:, t, :], pv), (6, 7)))
        fillers.append(tm_work("mv", Wm, 512, M2, evac(lambda t: mv[:, t, :], pv), (6, 7)))
        xt, ff_done, up_done, rows_done = ffn(1, xt, [xa_done], xa_done, 2, 0)

        X = norm_T(xr, xt, gain2(16), XTh, XTl, up_done, 2, 0)
        drain("mv")
        mkt, mvt = ready["mk"], ready["mv"]
        mem_done = pe_now()
        W = I["w_in_2"][0]
        kfree = [pv, ff_done, M2.toks]
        hq, hf, hk, hG = (reg(1024 * i, 1024).rearrange("p (h t) -> p h t", h=4) for i in range(4))
        KQ = [reg(4096, 1024), hf.rearrange("p h t -> p (h t)")]
        Am = reg(5120, 1024).rearrange("p (g t) -> p g t", g=8)
        A01 = reg(6144, 512).rearrange("p (h t) -> p h t", h=4)
        hi = reg(6656, 1024).rearrange("p (t d) -> p t d", t=2)
        hg = reg(7680, 1024).rearrange("p (t d) -> p t d", t=2)
        fq, fk, fv, mq = (reg(8704 + 1024 * i, 1024).rearrange("p (t d) -> p t d", t=2) for i in range(4))

        def sig(i, t):
            return grow[:, i, 512 * t:512 * t + 512] if i < 4 else xn[:, t, 512 * (i - 4):512 * (i - 4) + 512]

        l0, l1 = gcol[:, 136:140], gcol[:, 140:144]
        mx, e01, lsum, lb, oml = stat(4), stat(8), stat(4), stat(4), stat(4)
        c = V("tensor_tensor", mx, l0, l1, ALU.max, w=gt[1])
        c1 = V("tensor_tensor", e01[:, 0:4], l0, mx, ALU.subtract, w=c)
        c2 = V("tensor_tensor", e01[:, 4:8], l1, mx, ALU.subtract, w=c)
        c = A(e01, e01, ACT.Exp, w=[c1, c2])
        c = V("tensor_tensor", lsum, e01[:, 0:4], e01[:, 4:8], ALU.add, w=c)
        c = V("reciprocal", lsum, lsum, w=c)
        c = V("tensor_tensor", lb, e01[:, 0:4], lsum, ALU.mult, w=c)
        c_lb = V("tensor_scalar", oml, lb, -1.0, 1.0, ALU.mult, ALU.add, w=c)

        hqt = []
        for i in range(2):
            b, t = fm_chunk([W[:, 0 + 256 * i:256 + 256 * i]], X)
            e = A(hq[:, 2 * i:2 * i + 2, :], ps[:, b, :].rearrange("p (a c) -> p a c", a=2), ACT.Silu, w=[t, kfree])
            bfree[b] = [e]
            hqt.append(e)
        hft = []
        for i in range(2):
            b, t = fm_chunk([W[:, 512 + 256 * i:768 + 256 * i]], X)
            e = A(hf[:, 2 * i:2 * i + 2, :], ps[:, b, :].rearrange("p (a c) -> p a c", a=2), ACT.Sigmoid, w=[t, kfree])
            bfree[b] = [e]
            hft.append(e)
        fts = []
        for h in range(4):
            e = V("tensor_scalar", hf[:, h, :], hf[:, h, :], oml[:, h:h + 1], lb[:, h:h + 1], ALU.mult, ALU.add,
                  w=[hft[h // 2], c_lb])
            fts.append(e)
        hkt = V("tensor_scalar", hk, hf, -1.0, 1.0, ALU.mult, ALU.add, w=[fts, kfree])
        e = A(hf, hf, ACT.Ln, w=[fts, hkt])
        gts = []
        for h in range(4):
            for t in range(NT):
                gts.append(V("tensor_tensor_scan", hG[:, h, 128 * t:128 * t + 128], onesf[:, 0:128],
                             hf[:, h, 128 * t:128 * t + 128], 0.0, ALU.mult, ALU.add, w=[e, c_ones, kfree]))
        G8 = hG.rearrange("p h (t c) -> p (h t) c", t=2)
        NF = (2, 1, 1, 1, 1, 1, 1, 0)
        azero = V("memset", Am, 0.0, w=kfree)

        fl, fc = reg(12800, 248 + 8)[0:8, :], fcr[:, :]

        def fox_gates():
            b, t = gate_rows(W, 3584, 8, 1, X)
            u = V("tensor_scalar", fl, ps[0:8, b, 0:256], gb[0:8, 2:3], None, ALU.add, w=[t, l_gb, kfree])
            bfree[b] = [u]
            n = V("scalar_tensor_tensor", fc, fl, -1.0, fl, ALU.mult, ALU.min, w=u)
            n = A(fc, fc, ACT.Exp, w=n)
            n = A(fc, fc, ACT.Ln, bias=1.0, w=n)
            n = V("scalar_tensor_tensor", fl, fl, 0.0, fc, ALU.min, ALU.subtract, w=[n, u])
            n = V("tensor_tensor_scan", fc, onesf[0:8, :], fl, 0.0, ALU.mult, ALU.add, w=[n, c_ones])
            ready["fc"] = n
            ready["fl"] = V("tensor_scalar", fl, fc, -1.0, None, ALU.mult, w=n)
            yield False

        def gate_work(i):
            return tm_work(("gate", i), W, 4104 + 512 * i, X, through(lambda t: sig(i, t), ACT.Sigmoid, [rows_done, xn_free]))

        fillers.append(tm_work("hi", W, 1024, X, evac(lambda t: hi[:, t, :], kfree)))
        fillers.append(tm_work("hg", W, 1536, X, through(lambda t: hg[:, t, :], ACT.Silu, kfree)))
        fillers.append(tm_work("fq", W, 2048, X, evac(lambda t: fq[:, t, :], kfree)))
        fillers.append(tm_work("fk", W, 2560, X, evac(lambda t: fk[:, t, :], kfree)))
        fillers.append(fox_gates())
        fillers.append(tm_work("fv", W, 3072, X, evac(lambda t: fv[:, t, :], kfree)))
        fillers.append(tm_work("mq", W, 3592, X, evac(lambda t: mq[:, t, :], kfree)))
        fillers += [gate_work(i) for i in range(6)]

        mtok = {}
        ktok = {}
        pred = [azero]
        for i in range(8):
            bk = 4 + 2 * (i % 2)
            if i < 7:
                L = 1 << i
                nb = 512 // L
                kq = KQ[i % 2]
                v = kq.rearrange("p (b h l) -> p b h l", h=2, l=L)
                gv = reg(3072, 1024).rearrange("p (b h l) -> p b h l", h=2, l=L)
                qv = reg(0, 1024).rearrange("p (b h l) -> p b h l", h=2, l=L)
                kv = reg(2048, 1024).rearrange("p (b h l) -> p b h l", h=2, l=L)
                gr = reg(3072, 1024).rearrange("p (b c) -> p b c", c=2 * L)
                d = V("tensor_tensor", kq.rearrange("p (b c) -> p b c", c=2 * L), gr,
                      gr[:, :, L - 1:L].to_broadcast([128, nb, 2 * L]), ALU.subtract, w=[gts, ktok.get(i - 2), kfree])
                ea = A(v[:, :, 0, :], v[:, :, 0, :], ACT.Exp, scale=-1.0, w=d)
                eb = A(v[:, :, 1, :], v[:, :, 1, :], ACT.Exp, w=d)
                m1_ = V("tensor_tensor", v[:, :, 0, :], v[:, :, 0, :], kv[:, :, 0, :], ALU.mult, w=[ea, hkt])
                m2_ = V("tensor_tensor", v[:, :, 1, :], v[:, :, 1, :], qv[:, :, 1, :], ALU.mult, w=[eb, hqt])
                src = [(kq[:, 128 * g:128 * g + 128], kq[:, 128 * g:128 * g + 128]) for g in range(8)]
                wt = [m1_, m2_]
            else:
                k8 = hk.rearrange("p h (t c) -> p (h t) c", t=2)
                q8 = hq.rearrange("p h (t c) -> p (h t) c", t=2)
                src = [(k8[:, g, :], q8[:, g, :]) for g in range(8)]
                wt = [hkt, hqt]
            fill(NF[i], False)
            for g in range(8):
                m = T(ps[:, bk + g // 4, 128 * (g % 4):128 * (g % 4) + 128], src[g][0], src[g][1], start=True, stop=True,
                      w=[wt, bfree[bk + g // 4] if g % 4 == 0 else None], inc=g == 7)
            ktok[i] = m
            e = V("copy_predicated", Am, lvl[:, i, :].unsqueeze(1).to_broadcast([128, 8, 128]),
                  ps[:, bk:bk + 2, :].rearrange("p b (g t) -> p (b g) t", g=4), w=[m, c_lvl, pred[-1]])
            pred.append(e)
            bfree[bk] = bfree[bk + 1] = [e]
        kq = KQ[0].rearrange("p (h t c) -> p h t c", h=4, t=2)
        G4 = hG.rearrange("p h (t c) -> p h t c", t=2)
        d1 = V("tensor_tensor", kq[:, :, 0, :], G4[:, :, 0, :], G4[:, :, 0, 127:128].to_broadcast([128, 4, 128]), ALU.subtract,
               w=[gts, ktok[6]])
        ea = A(kq[:, :, 0, :], kq[:, :, 0, :], ACT.Exp, scale=-1.0, w=d1)
        eb = A(kq[:, :, 1, :], G4[:, :, 1, :], ACT.Exp, w=[gts, ktok[6]])
        m1_ = V("tensor_tensor", kq[:, :, 0, :], kq[:, :, 0, :], hk.rearrange("p h (t c) -> p h t c", t=2)[:, :, 0, :], ALU.mult, w=ea)
        m2_ = V("tensor_tensor", kq[:, :, 1, :], kq[:, :, 1, :], hq.rearrange("p h (t c) -> p h t c", t=2)[:, :, 1, :], ALU.mult, w=eb)
        drain("hi")
        drain("hg")
        fill(1, False)
        hit, hgt = ready["hi"], ready["hg"]
        for h in range(4):
            m = T(ps[:, 4, 128 * h:128 * h + 128], kq[:, h, 0, :], kq[:, h, 1, :], start=True, stop=True,
                  w=[m1_, m2_, bfree[4]], inc=h == 3)
        a01 = A(A01.rearrange("p h t -> p (h t)"), ps[:, 4, :], ACT.Copy, w=[m, kfree])
        bfree[4] = [a01]
        zt = []
        for t in range(NT):
            bk = 6 + t
            for h in range(4):
                o = ps[:, bk, 128 * h:128 * h + 128]
                iv = lambda s: hi[:, s, 128 * h:128 * h + 128]
                if t == 0:
                    m = T(o, Am[:, 2 * h, :], iv(0), start=True, stop=True, w=[pred[-1], hit, bfree[bk]], inc=h == 3)
                else:
                    T(o, A01[:, h, :], iv(0), start=True, stop=False, w=[a01, bfree[bk]])
                    m = T(o, Am[:, 2 * h + 1, :], iv(1), start=False, stop=True, inc=h == 3)
            o4 = ps[:, bk, :].rearrange("p (h d) -> p h d", h=4)
            sq = KQ[1][:, 512 * t:512 * t + 512]
            ss = stat(4)
            s = A(sq, ps[:, bk, :], ACT.Square, w=[m, ktok[6]])
            s = V("tensor_reduce", ss, sq.rearrange("p (h d) -> p h d", h=4), AX.X, ALU.add, w=s)
            r, rt = rstd(ss, 4, 128, s)
            e = V("tensor_tensor", sq.rearrange("p (h d) -> p h d", h=4), o4, r.unsqueeze(2).to_broadcast([128, 4, 128]), ALU.mult,
                  w=[rt, s])
            bfree[bk] = [e]
            zt.append(V("tensor_tensor", hg[:, t, :], hg[:, t, :], sq, ALU.mult, w=[e, hgt]))
        yah, yal, ybh, ybl, ych, ycl = (rr(4096 + 1024 * i, 4) for i in range(6))
        drain("fk")
        fqt, fkt = ready["fq"], ready["fk"]
        fill(1, False)
        g, gw = gain2(48, 1)
        yat, tr_a = turn(hg, 4, zt, yah, yal, lambda k: (g, gw), mem_done, banks=(4, 5))
        hg_done = [tr_a, ktok[7], pe_now(), zt]

        def head_norm(src, toks, nh, sqr, sqfree):
            dh = 512 // nh
            res = []
            for t in range(NT):
                ss = stat(nh)
                s = A(sqr[:, 512 * t:512 * t + 512], src[:, t, :], ACT.Square, w=[toks[t], sqfree])
                s = V("tensor_reduce", ss, sqr[:, 512 * t:512 * t + 512].rearrange("p (h d) -> p h d", h=nh), AX.X, ALU.add, w=s)
                r, rt = rstd(ss, nh, dh, s)
                sv = src[:, t, :].rearrange("p (h d) -> p h d", h=nh)
                res.append(V("tensor_tensor", sv, sv, r.unsqueeze(2).to_broadcast([128, nh, dh]), ALU.mult, w=rt))
            return res

        mkT = reg(3072, 1024).rearrange("p (k t) -> p k t", k=4)
        mqT = reg(4096, 1024).rearrange("p (k t) -> p k t", k=4)
        fqT = Kx[:, 0:4, :]
        fkT = Kx[:, 4:8, :]
        sqa = reg(7680, 1024)
        gq8 = stat(1)
        gq8t = V("tensor_scalar", gq8, gcol[:, 147:148], 0.125, None, ALU.mult, w=gt[1])
        n = head_norm(fq, fqt, 8, sqa, [m, hg_done])
        fill(1, False)
        fqTt, _ = turn(fq, 4, n, fqT, None, lambda k: (gq8, gq8t), [kfree, hg_done], banks=(6, 7))
        n = head_norm(fk, fkt, 8, sqa, None)
        fill(1, False)
        fkTt, _ = turn(fk, 4, n, fkT, None, lambda k: gain2(52, 1), [kfree, hg_done], banks=(4, 5))
        n = head_norm(mk, mkt, 4, sqa, None)
        fill(1, False)
        mkTt, _ = turn(mk, 4, n, mkT, None, lambda k: gain2(50, 1), [mem_done, hg_done], banks=(6, 7))
        drain("mq")
        fvt, mqt = ready["fv"], ready["mq"]
        n5, n6 = ready["fc"], ready["fl"]
        n = head_norm(mq, mqt, 4, sqa, None)
        fill(1, False)
        mqTt, _ = turn(mq, 4, n, mqT, None, lambda k: gain2(49, 1), [mem_done, hg_done], banks=(4, 5))
        for t in range(NT):
            tc = TR(ps[:, 6, 8 * t:8 * t + 8], fc[:, 128 * t:128 * t + 128], ident[0:8, 0:8], w=[n5, bfree[6]], inc=t == 1)
        fcc = stat(16)
        fct = V("tensor_copy", fcc, ps[:, 6, 0:16], w=tc)
        bfree[6] = [fct]

        mg = reg(8704, 2048).rearrange("p (t d) -> p t d", t=2)
        bt = reg(10752, 1024)
        mtok = [[None, None], [None, None]]
        Ya = Split(yah, yal, yat)
        NM = (0, 1, 1, 1, 1, 1, 1)

        def merge(br, half, Y):
            nm = ("w_br_hgrn_2", "w_br_fox_2", "w_br_mem_2")[br]
            for pr, toks in tm_steps(I[nm][0], 512 * half, Y):
                yield toks is None
            gw = ready[("gate", 2 * br + half)]
            for t in range(NT):
                gsl = sig(2 * br + half, t)
                dst = mg[:, t, 512 * half:512 * half + 512]
                if br == 0:
                    e = V("tensor_tensor", dst, ps[:, pr[t], :], gsl, ALU.mult, w=[toks[t], gw[t], hg_done, fqTt, fkTt])
                    bfree[pr[t]] = [e]
                else:
                    tmp = bt[:, 512 * t:512 * t + 512]
                    e = V("tensor_tensor", tmp, ps[:, pr[t], :], gsl, ALU.mult, w=[toks[t], gw[t], ptf, mtok[t]])
                    bfree[pr[t]] = [e]
                    e = V("tensor_tensor", dst, dst, tmp, ALU.add, w=[e, mtok[t][half]])
                mtok[t][half] = e

        Pf = reg(0, 1536).rearrange("p (h c) -> p h c", h=4)
        PTf = reg(1536, 1536).rearrange("p (h c) -> p h c", h=4)
        pvf = [hg_done]
        ptf = [hg_done]
        ybt = []
        for g in range(2):
            for h4 in range(4):
                h = 4 * g + h4
                bk = 4 + h4
                r = slice(64 * (h % 2), 64 * (h % 2) + 64)
                T(ps[:, bk, 0:128], identb[:, :], mRow[:, :], start=True, stop=False, w=[bfree[bk]], skip_group_check=True)
                T(ps[:, bk, 256:384], identb[:, :], mRow[:, :], start=False, stop=False, skip_group_check=True)
                sel = ident[0:8, h:h + 1].to_broadcast([8, 128])
                T(ps[:, bk, 0:128], sel, fl[:, 0:128], start=False, stop=False, w=n6, skip_group_check=True)
                T(ps[:, bk, 128:384], sel, fl, start=False, stop=False, skip_group_check=True)
                T(ps[:, bk, 0:128], fqT[r, h // 2, 0:128], fkT[r, h // 2, 0:128], start=False, stop=False, w=[fqTt, fkTt],
                  skip_group_check=True)
                m = T(ps[:, bk, 128:384], fqT[r, h // 2, 128:256], fkT[r, h // 2, :], start=False, stop=True,
                      skip_group_check=True, inc=True)
            mx, sm, ri = stat(8), stat(8), stat(8)
            cols = (slice(0, 128), slice(128, 384))
            nrm = []
            for t in range(NT):
                fcol = fcc[:, 8 * t + 4 * g:8 * t + 4 * g + 4]
                e = V("tensor_reduce", mx[:, 4 * t:4 * t + 4], ps[:, 4:8, cols[t]], AX.X, ALU.max, w=m)
                e = V("tensor_tensor", mx[:, 4 * t:4 * t + 4], mx[:, 4 * t:4 * t + 4], fcol, ALU.add, w=[e, fct])
                nrm.append(V("tensor_tensor", mx[:, 4 * t:4 * t + 4], fcol, mx[:, 4 * t:4 * t + 4], ALU.subtract, w=e))
            for h4 in range(4):
                for t in range(NT):
                    e = A(Pf[:, h4, cols[t]], ps[:, 4 + h4, cols[t]], ACT.Exp, bias=mx[:, 4 * t + h4:4 * t + h4 + 1],
                          accum_out=sm[:, 4 * t + h4:4 * t + h4 + 1], w=[nrm, pvf])
                bfree[4 + h4] = [e]
            e = V("reciprocal", ri, sm, w=e)
            for t in range(NT):
                pn = V("tensor_tensor", Pf[:, :, cols[t]], Pf[:, :, cols[t]],
                       ri[:, 4 * t:4 * t + 4].unsqueeze(2).to_broadcast([128, 4, 128 * (t + 1)]), ALU.mult, w=e)
            fill(2, False)
            tl = []
            for h4 in range(4):
                bk = 4 + h4
                for i in range(3):
                    m = TR(ps[:, bk, 128 * i:128 * i + 128], Pf[:, h4, 128 * i:128 * i + 128], ident[:, :],
                           w=[pn, bfree[bk]], inc=i == 2)
                e = put("act" if h4 % 2 == 0 else "dve", PTf[:, h4, :], ps[:, bk, 0:384], [m, ptf])
                bfree[bk] = [e]
                tl.append(e)
            pvf = [m]
            for h4 in range(4):
                h = 4 * g + h4
                c = 256 * (h4 // 2)
                o = ps[64 * (h % 2):64 * (h % 2) + 64, 4, :]
                T(o[:, c:c + 256], fv[:, 0, 64 * h:64 * h + 64], PTf[:, h4, 0:256], start=True, stop=False,
                  w=[tl, fvt, bfree[4]], skip_group_check=True)
                m = T(o[:, c + 128:c + 256], fv[:, 1, 64 * h:64 * h + 64], PTf[:, h4, 256:384], start=False, stop=True,
                      skip_group_check=True, inc=h4 == 3)
            ptf = [m]
            e = put_split(ybh[:, 2 * g:2 * g + 2, :], ybl[:, 2 * g:2 * g + 2, :], ps[:, 4, :].rearrange("p (a c) -> p a c", a=2),
                          m, mem_done)
            bfree[4] = [e]
            ybt += [e, e]

        Y = Split(ych, ycl, [])
        fillers += [merge(0, 0, Ya), merge(0, 1, Ya), merge(1, 0, Split(ybh, ybl, ybt)), merge(1, 1, Split(ybh, ybl, ybt))]
        for i, stage in memory_attention(1, lambda h: (mqT[:, h:h + 1, :], mqTt[h]), lambda h: mkT[:, h:h + 1, :],
                                         lambda h: mkTt[h], mv, lambda h: mvt, 128.0 ** -0.5, 5120, [hg_done, n], ych, ycl,
                                         lambda: mem_done, Y.toks):
            if stage == 0:
                fill(NM[i])
        fill(100)
        for half in range(2):
            for _ in merge(2, half, Y):
                pass
        br_done = pe_now()
        mTt, _ = turn(mg, 8, mtok, XTh, XTl, lambda k: (1.0, None), br_done)
        yt = out_proj(I["w_out_2"][0], Split(XTh, XTl, mTt))
        wo_done = pe_now()
        new = []
        for t in range(NT):
            e = V("tensor_tensor", xr[:, t, :].rearrange("p (h c) -> p h c", h=2), xr[:, t, :].rearrange("p (h c) -> p h c", h=2),
                  ps[:, 2 * t:2 * t + 2, :], ALU.add, w=[yt[t], xt[t]])
            bfree[2 * t] = bfree[2 * t + 1] = [e]
            new.append(e)
        xt = new
        xn_free[:] = [mtok[0], mtok[1]]

        X = norm_T(xr, xt, gain2(32), XTh, XTl, wo_done)

        def taps(j, k):
            return gcol[:, 149 + 22 * j + k:150 + 22 * j + k]

        def conv_gelu(j, b, tok, tmp, w):
            tmp = tmp.rearrange("p (a t) -> p a t", a=2)
            a4 = ps[:, b, :].rearrange("p (a t) -> p a t", a=2)
            es = []
            for i in range(2):
                k = 2 * j + i
                a = A(tmp[:, i, :], a4[:, i, :], ACT.Identity, scale=taps(2, k), bias=taps(3, k), w=[tok, gt[2], w])
            for i in range(2):
                k = 2 * j + i
                e = V("scalar_tensor_tensor", tmp[:, i, 1:256], a4[:, i, 0:255], taps(1, k), tmp[:, i, 1:256], ALU.mult, ALU.add, w=a)
                e = V("scalar_tensor_tensor", tmp[:, i, 2:256], a4[:, i, 0:254], taps(0, k), tmp[:, i, 2:256], ALU.mult, ALU.add, w=e)
                es.append(e)
            bfree[b] = [e]
            return A(tmp, tmp, ACT.Gelu, w=es)

        yt, _ = feed_forward(I["ffn_w_up_2"][0], I["ffn_w_down_2"][0], X, conv_gelu, [br_done, mtok])
        o2 = out.rearrange("o (t p) d -> p (o t) d", p=128)
        s_out = sem("s_out")
        for t in range(NT):
            e = V("tensor_tensor", xr[:, t, :].rearrange("p (h c) -> p h c", h=2), xr[:, t, :].rearrange("p (h c) -> p h c", h=2),
                  ps[:, 2 * t:2 * t + 2, :], ALU.add, w=[yt[t], xt[t]])
            sp.put("dma_start", (o2[:, t, :], xr[:, t, :]), {}, flat(e), inc=s_out, by=16)
        sp.put(None, (), {}, [(s_out, 32)])

        block = ctx.enter_context(nc.Block())

        @block.sync
        def _(e):
            sp.run(e)

        @block.scalar
        def _(e):
            act.run(e)

        @block.vector
        def _(e):
            dve.run(e)

        @block.gpsimd
        def _(e):
            pool.run(e)

        @block.tensor
        def _(e):
            pe.run(e)


_INS = ["x", "mem", "mem_norm_gain", "norm_gains", "ml_w_in", "ml_b_gate", "ml_head_gain", "ml_w_out", "sb_w_qkv",
        "sb_w_out", "xa_w_q", "xa_w_kv", "xa_w_o", "ffn_w_gate_up", "ffn_w_down", "mem_2", "norm_mix_g_2",
        "norm_mem_g_2", "w_in_2", "hgrn_lb_logits_2", "hgrn_norm_g_2", "fox_f_bias_2", "fox_q_norm_g_2",
        "fox_k_norm_g_2", "mem_kv_w_2", "mem_q_norm_g_2", "mem_k_norm_g_2", "w_br_hgrn_2", "w_br_fox_2",
        "w_br_mem_2", "w_out_2", "norm_ffn_g_2", "ffn_w_up_2", "ffn_conv_w_2", "ffn_conv_b_2", "ffn_w_down_2"]


def kernel(**inputs):
    import numpy as _np
    import concourse.bacc as _bacc
    from concourse.bass_utils import run_bass_kernel_spmd as _run

    nc = _bacc.Bacc("TRN2", target_bir_lowering=False, num_devices=1)
    arrays, aps = {}, {}
    for name in _INS:
        a = _np.ascontiguousarray(inputs[name])
        arrays[f"in_{name}"] = a
        aps[name] = nc.dram_tensor(f"in_{name}", a.shape, mybir.dt.from_np(a.dtype), kind="ExternalInput").ap()
    out = nc.dram_tensor("out_0", (1, 256, 1024), F32, kind="ExternalOutput").ap()
    build_program(nc, aps, out)
    r = _run(nc, [arrays], core_ids=[0])
    return r.results[0]["out_0"]
```
